# Optimizing a Trainium2 kernel written in Bass

```python
import math
import jax, jax.numpy as jnp
from jax import lax
import numpy as np

D_MODEL = 1024
BATCH = 1
SEQ = 512
DEPTH = 2

N_MIXERS = 2
N_RWKV_LAYERS = (DEPTH + 1) // 2
N_ATTN_LAYERS = DEPTH // 2

RWKV_HEAD_SIZE = 64
RWKV_HEADS = D_MODEL // RWKV_HEAD_SIZE
RWKV_DECAY_LORA = max(32, int(round(1.8 * D_MODEL ** 0.5 / 32)) * 32)
RWKV_AAA_LORA = max(32, int(round(1.8 * D_MODEL ** 0.5 / 32)) * 32)
RWKV_MV_LORA = max(32, int(round(1.3 * D_MODEL ** 0.5 / 32)) * 32)
RWKV_GATE_LORA = max(32, int(round(0.6 * D_MODEL ** 0.8 / 32)) * 32)
RWKV_LN_EPS = 64e-5

ATTN_HEAD_DIM = 64
ATTN_HEADS = D_MODEL // ATTN_HEAD_DIM
DILATION_PAIRS = ((128, 1), (512, 4), (2048, 16))
N_GROUPS = len(DILATION_PAIRS)
BAND_BLOCK = max(w // d for w, d in DILATION_PAIRS)
NUM_BUCKETS = 32
MAX_DISTANCE = max(w for w, _ in DILATION_PAIRS)
NEG_INF = -1e30

D_FF = -(-8 * D_MODEL // (3 * 256)) * 256
RMS_EPS = 1e-6

kernel_name = "hybrid_rwkv7_dilated_attn_trunk"

def rms_norm(x, gain, eps=RMS_EPS):
    xf = x.astype(jnp.float32)
    y = xf * lax.rsqrt(jnp.mean(xf * xf, axis=-1, keepdims=True) + eps)
    return (y * gain).astype(x.dtype)

def swiglu_ffn(h, w_in, w_out):
    gate, up = jnp.split(h @ w_in, 2, axis=-1)
    return (jax.nn.silu(gate) * up) @ w_out

def rwkv7_scan(r, decay, k, v, a_vec, b_vec):
    B, S, H, N = r.shape

    def step(state, inp):
        r_t, w_t, k_t, v_t, a_t, b_t = inp
        sa = jnp.einsum('bhij,bhj->bhi', state, a_t)
        state = (state * w_t[:, :, None, :] + sa[..., None] * b_t[:, :, None, :]
                 + v_t[..., None] * k_t[:, :, None, :])
        return state, jnp.einsum('bhij,bhj->bhi', state, r_t)

    xs = tuple(jnp.swapaxes(t, 0, 1) for t in (r, decay, k, v, a_vec, b_vec))
    _, y = lax.scan(step, jnp.zeros((B, H, N, N), jnp.float32), xs)
    return jnp.swapaxes(y, 0, 1)

def rwkv7_time_mix(h, v_first, mu, w_rkv, w0, w1, w2, a0, a1, a2, g1, g2,
                   k_k, k_a, r_k, ln_w, ln_b, w_o, v_gate):
    B, S, D = h.shape
    H, N = RWKV_HEADS, RWKV_HEAD_SIZE

    def heads(t):
        return t.reshape(B, S, H, N).astype(jnp.float32)

    xx = jnp.pad(h, ((0, 0), (1, 0), (0, 0)))[:, :-1] - h
    x_mix = h[None] + xx[None] * mu[:, None, None, :]
    rkv = jnp.einsum('cbsd,cde->cbse', x_mix[:3], w_rkv)
    r, k, v = rkv[0], rkv[1], rkv[2]
    xw, xa, xg, xv = x_mix[3], x_mix[4], x_mix[5], x_mix[2]

    w = -jax.nn.softplus(-(w0 + jnp.tanh(xw @ w1) @ w2)) - 0.5
    decay = jnp.exp(-jnp.exp(w.astype(jnp.float32)))
    a = jax.nn.sigmoid(a0 + (xa @ a1) @ a2)
    g = jax.nn.sigmoid(xg @ g1) @ g2
    if v_gate is None:
        v_first = v
    else:
        v0, v1, v2 = v_gate
        v = v + (v_first - v) * jax.nn.sigmoid(v0 + (xv @ v1) @ v2)

    kk = heads(k * k_k)
    kk = kk * lax.rsqrt(jnp.maximum(jnp.sum(kk * kk, axis=-1, keepdims=True), 1e-24))
    k = k * (1.0 + (a - 1.0) * k_a)
    rh, kh, vh, ah = heads(r), heads(k), heads(v), heads(a)
    y = rwkv7_scan(rh, decay.reshape(B, S, H, N), kh, vh, -kk, kk * ah)

    mean = jnp.mean(y, axis=-1, keepdims=True)
    var = jnp.mean(jnp.square(y - mean), axis=-1, keepdims=True)
    y = ((y - mean) * lax.rsqrt(var + RWKV_LN_EPS)).reshape(B, S, D) * ln_w + ln_b
    r_k_h = r_k.reshape(H, N).astype(jnp.float32)
    bonus = jnp.sum(rh * kh * r_k_h, axis=-1, keepdims=True) * vh
    out = ((y + bonus.reshape(B, S, D)) * g).astype(h.dtype) @ w_o
    return out, v_first

def t5_bucket(dist):
    max_exact = NUM_BUCKETS // 2
    large = max_exact + (jnp.log(jnp.maximum(dist, 1).astype(jnp.float32) / max_exact)
                         / math.log(MAX_DISTANCE / max_exact)
                         * (NUM_BUCKETS - max_exact)).astype(jnp.int32)
    large = jnp.minimum(large, NUM_BUCKETS - 1)
    return jnp.where(dist < max_exact, dist, large)

def band_bias(table_g, window, dilation):
    blk = BAND_BLOCK
    i = jnp.arange(blk)[:, None]
    c = jnp.arange(2 * blk)[None, :]
    steps = i + blk - c
    allowed = (steps >= 0) & (steps <= window // dilation)
    bucket = t5_bucket(jnp.maximum(steps, 0) * dilation)
    bias = jnp.take(table_g, bucket, axis=0).astype(jnp.float32)
    bias = jnp.where(allowed[..., None], bias, NEG_INF)
    return jnp.transpose(bias, (2, 0, 1))

def dilated_band_attention(q, k, v, bias, dilation):
    B, S, H, Dh = q.shape
    blk = BAND_BLOCK
    span = blk * dilation
    s_pad = -(-S // span) * span
    nb = s_pad // span

    def to_blocks(t):
        t = jnp.pad(t, ((0, 0), (0, s_pad - S), (0, 0), (0, 0)))
        return t.reshape(B, nb, blk, dilation, H, Dh)

    def band(t):
        prev = jnp.concatenate([jnp.zeros_like(t[:, :1]), t[:, :-1]], axis=1)
        return jnp.concatenate([prev, t], axis=2)

    qb = to_blocks(q)
    kband, vband = band(to_blocks(k)), band(to_blocks(v))
    logits = jnp.einsum('bnirhe,bncrhe->bnrhic', qb, kband).astype(jnp.float32)
    logits = logits + bias[None, None, None]
    key_ok = (jnp.arange(nb)[:, None] > 0) | (jnp.arange(2 * blk)[None, :] >= blk)
    logits = jnp.where(key_ok[None, :, None, None, None, :], logits, NEG_INF)
    lse = jax.nn.logsumexp(logits, axis=-1)
    probs = jnp.exp(logits - lse[..., None]).astype(v.dtype)
    out = jnp.einsum('bnrhic,bncrhe->bnirhe', probs, vband).reshape(B, s_pad, H, Dh)[:, :S]
    lse = jnp.transpose(lse, (0, 1, 4, 2, 3)).reshape(B, s_pad, H)[:, :S]
    return out, lse

def dilated_attention_mixer(h, w_qkv, q_gain, k_gain, w_o, rel_bias):
    B, S, _ = h.shape
    qkv = (h @ w_qkv).reshape(B, S, N_GROUPS, 3, ATTN_HEADS, ATTN_HEAD_DIM)
    scale = ATTN_HEAD_DIM ** -0.5
    outs, lses = [], []
    for g, (window, dilation) in enumerate(DILATION_PAIRS):
        q = rms_norm(qkv[:, :, g, 0], q_gain[g]) * scale
        k = rms_norm(qkv[:, :, g, 1], k_gain[g])
        v = qkv[:, :, g, 2]
        bias = band_bias(rel_bias[:, g * ATTN_HEADS:(g + 1) * ATTN_HEADS], window, dilation)
        o, l = dilated_band_attention(q, k, v, bias, dilation)
        outs.append(o)
        lses.append(l)
    weights = jax.nn.softmax(jnp.stack(lses), axis=0)
    o = jnp.sum(weights[..., None] * jnp.stack(outs).astype(jnp.float32), axis=0)
    return o.reshape(B, S, ATTN_HEADS * ATTN_HEAD_DIM).astype(h.dtype) @ w_o

def setup_inputs(seed: int = 0) -> dict:
    key = jax.random.key(seed)
    ks = iter(jax.random.split(key, 40))
    f32 = jnp.float32
    D, NR, NA = D_MODEL, N_RWKV_LAYERS, N_ATTN_LAYERS

    def nrm(shape, scale):
        return jax.random.normal(next(ks), shape, f32) * scale

    def gain(shape):
        return 1.0 + nrm(shape, 0.02)

    qkv_cols = N_GROUPS * 3 * ATTN_HEADS * ATTN_HEAD_DIM
    return {
        "x": nrm((BATCH, SEQ, D), 1.0),
        "mix_norm": gain((DEPTH, D)),
        "ffn_norm": gain((DEPTH, D)),
        "ffn_w_in": nrm((DEPTH, D, 2 * D_FF), D ** -0.5),
        "ffn_w_out": nrm((DEPTH, D_FF, D), D_FF ** -0.5),
        "rwkv_mu": jax.random.uniform(next(ks), (NR, 6, D), f32),
        "rwkv_w_rkv": nrm((NR, 3, D, D), D ** -0.5),
        "rwkv_w0": -6.0 + 5.0 * jax.random.uniform(next(ks), (NR, D), f32),
        "rwkv_w1": nrm((NR, D, RWKV_DECAY_LORA), D ** -0.5),
        "rwkv_w2": nrm((NR, RWKV_DECAY_LORA, D), 0.5 * RWKV_DECAY_LORA ** -0.5),
        "rwkv_a0": nrm((NR, D), 0.1),
        "rwkv_a1": nrm((NR, D, RWKV_AAA_LORA), D ** -0.5),
        "rwkv_a2": nrm((NR, RWKV_AAA_LORA, D), 0.5 * RWKV_AAA_LORA ** -0.5),
        "rwkv_v0": 1.0 + nrm((NR - 1, D), 0.1),
        "rwkv_v1": nrm((NR - 1, D, RWKV_MV_LORA), D ** -0.5),
        "rwkv_v2": nrm((NR - 1, RWKV_MV_LORA, D), 0.5 * RWKV_MV_LORA ** -0.5),
        "rwkv_g1": nrm((NR, D, RWKV_GATE_LORA), D ** -0.5),
        "rwkv_g2": nrm((NR, RWKV_GATE_LORA, D), RWKV_GATE_LORA ** -0.5),
        "rwkv_k_k": 0.85 + nrm((NR, D), 0.02),
        "rwkv_k_a": gain((NR, D)),
        "rwkv_r_k": nrm((NR, D), 0.1),
        "rwkv_ln_w": gain((NR, D)),
        "rwkv_ln_b": nrm((NR, D), 0.02),
        "rwkv_w_o": nrm((NR, D, D), D ** -0.5),
        "attn_w_qkv": nrm((NA, D, qkv_cols), D ** -0.5),
        "attn_q_gain": gain((NA, N_GROUPS, ATTN_HEAD_DIM)),
        "attn_k_gain": gain((NA, N_GROUPS, ATTN_HEAD_DIM)),
        "attn_w_o": nrm((NA, ATTN_HEADS * ATTN_HEAD_DIM, D), (ATTN_HEADS * ATTN_HEAD_DIM) ** -0.5),
        "rel_bias": nrm((NUM_BUCKETS, N_GROUPS * ATTN_HEADS), 0.5),
    }

def reference(x, mix_norm, ffn_norm, ffn_w_in, ffn_w_out, rwkv_mu, rwkv_w_rkv, rwkv_w0,
              rwkv_w1, rwkv_w2, rwkv_a0, rwkv_a1, rwkv_a2, rwkv_v0, rwkv_v1, rwkv_v2,
              rwkv_g1, rwkv_g2, rwkv_k_k, rwkv_k_a, rwkv_r_k, rwkv_ln_w, rwkv_ln_b, rwkv_w_o,
              attn_w_qkv, attn_q_gain, attn_k_gain, attn_w_o, rel_bias):
    v_first = None
    for layer in range(DEPTH):
        h = rms_norm(x, mix_norm[layer])
        idx = layer // N_MIXERS
        if layer % N_MIXERS == 0:
            v_gate = None if idx == 0 else (rwkv_v0[idx - 1], rwkv_v1[idx - 1], rwkv_v2[idx - 1])
            y, v_first = rwkv7_time_mix(
                h, v_first, rwkv_mu[idx], rwkv_w_rkv[idx], rwkv_w0[idx], rwkv_w1[idx], rwkv_w2[idx],
                rwkv_a0[idx], rwkv_a1[idx], rwkv_a2[idx], rwkv_g1[idx], rwkv_g2[idx],
                rwkv_k_k[idx], rwkv_k_a[idx], rwkv_r_k[idx], rwkv_ln_w[idx], rwkv_ln_b[idx],
                rwkv_w_o[idx], v_gate)
        else:
            y = dilated_attention_mixer(h, attn_w_qkv[idx], attn_q_gain[idx], attn_k_gain[idx],
                                        attn_w_o[idx], rel_bias)
        x = x + y
        x = x + swiglu_ffn(rms_norm(x, ffn_norm[layer]), ffn_w_in[layer], ffn_w_out[layer])
    return x


_drawn_inputs = setup_inputs


def setup_inputs(seed=0):
    import zlib

    import numpy as np

    out = dict(_drawn_inputs(seed))
    spreads = {}
    factors = {'ffn_norm': 2.899,
     'rwkv_w1': 4.439,
     'rwkv_w2': 4.42,
     'rwkv_k_k': 5.38,
     'rwkv_k_a': 4.609,
     'rwkv_ln_w': 4.639,
     'rwkv_ln_b': 4.511,
     'attn_q_gain': 8.0,
     'attn_k_gain': 8.0,
     'rel_bias': 4.882}
    for name, (base, spread) in spreads.items():
        noise = np.random.default_rng([zlib.crc32(name.encode()), seed]).standard_normal(out[name].shape)
        drawn = base * np.exp(spread * noise) if base else spread * noise
        out[name] = __import__('jax').numpy.asarray(drawn.astype(out[name].dtype))
    for name, factor in factors.items():
        out[name] = (out[name] * factor).astype(out[name].dtype)
    return out
```

```python
import math
from contextlib import ExitStack

import numpy as np

import concourse.bass as bass
from concourse import mybir

F32 = mybir.dt.float32
F32R = mybir.dt.float32r
ALU = mybir.AluOpType
ACT = mybir.ActivationFunctionType

P = 128
S = 512
D = 1024
KC = D // P
HD = 64
NHP = D // P
NT = S // P
CH = 64
NCH = S // CH
F = 2816
FC = F // P
LORA = 64
GLORA = 160
KAPPA = math.exp(-0.5)
NEG = -1e30

RAW = 2
PAN = 3
LEAD = PAN - 1

VECS = ["mix0", "ffn0", "mix1", "ffn1", "mu0", "mu1", "mu2", "mu3", "mu4", "mu5",
        "w0", "a0", "k_k", "k_a", "r_k", "ln_w", "ln_b"]
PAN_R, PAN_W, PAN_K, PAN_A, PAN_V, PAN_G = 0, 8, 9, 17, 18, 26
PAN_WO0 = 28
PAN_IN0 = PAN_WO0 + KC
PAN_OUT0 = PAN_IN0 + 2 * FC
PAN_QKV = PAN_OUT0 + FC
PAN_WO1 = PAN_QKV + 9 * NHP
PAN_IN1 = PAN_WO1 + KC
PAN_OUT1 = PAN_IN1 + 2 * FC
N_PAN = PAN_OUT1 + FC

C_ID, C_ONES, C_HEAD, C_MEAN = 0, 128, 256, 384
C_STRICT, C_INCL = 512, 640
C_LEV = 768
N_LEV = 6
C_LEVT = C_LEV + N_LEV * 128
C_RESET = C_LEVT + 128
C_OH = C_RESET + 512
N_CONST = C_OH + 3 * 384


def shape_constants():
    c = np.zeros((P, N_CONST), np.float32)
    i = np.arange(P)
    same = lambda m: (i[:, None] // m) == (i[None, :] // m)
    c[:, C_ID:C_ID + P] = np.eye(P)
    c[:, C_ONES:C_ONES + P] = 1.0
    c[:, C_HEAD:C_HEAD + P] = same(HD)
    c[:, C_MEAN:C_MEAN + P] = same(HD) / float(HD)
    c[:, C_STRICT:C_STRICT + P] = -1.0 * (same(CH) & (i[:, None] < i[None, :]))
    c[:, C_INCL:C_INCL + P] = same(CH) & (i[:, None] <= i[None, :])
    for n in range(N_LEV):
        m = 1 << n
        low = same(2 * m) & ((i[:, None] // m) % 2 == 1) & ((i[None, :] // m) % 2 == 0)
        lev = (low | (i[:, None] == i[None, :])).astype(np.float32)
        c[:, C_LEV + n * P:C_LEV + (n + 1) * P] = lev
        if n == 0:
            c[:, C_LEVT:C_LEVT + P] = lev.T
    c[:, C_RESET:C_RESET + S] = (np.arange(S) % CH != 0)[None, :]
    u = np.arange(384)
    for g in range(3):
        if g == 0:
            steps, dist, ok = 255 - u, 255 - u, (255 - u >= 0) & (255 - u <= 128)
        elif g == 1:
            steps = 127 - u
            dist, ok = steps * 4, steps >= 0
        else:
            steps = 127 - u
            dist, ok = steps * 4, (steps >= 0) & (steps % 4 == 0)
        far = np.maximum(dist, 1).astype(np.float32)
        large = 16 + (np.log(far / np.float32(16)) / np.float32(math.log(2048 / 16)) * np.float32(16)).astype(np.int32)
        bucket = np.where(dist < 16, dist, np.minimum(large, 31))
        at = C_OH + g * 384
        for n in range(384):
            if ok[n]:
                c[bucket[n], at + n] = 1.0
            else:
                c[32, at + n] = NEG
    return c


def bc(ap, *dims):
    return bass.AP(tensor=ap.tensor, offset=ap.offset, ap=[list(ap.ap[0])] + [list(d) for d in dims])


O_RAW = 0
O_WHI = O_RAW + RAW * 1024
O_WLO = O_WHI + PAN * 1024
O_CON = O_WLO + PAN * 1024
O_PV = O_CON + 512
N_PV = len(VECS) * KC + 6 + 5
O_SM = O_PV + 160
O_RSTD = O_SM + 96
O_X = O_RSTD + S
O_A = O_X + KC * S
O_B = O_A + 2 * KC * S
TOTAL = 53120
K_EPS, K_LNEPS, K_KKB, K_ONE, K_ZERO = range(len(VECS) * KC + 6, N_PV)
O_TW = O_B
O_TA = O_TW + S
O_TG = O_TA + S
O_C1 = O_TG + 2 * S
O_H = O_C1
O_XX = O_H + KC * (S + 1)
O_XM = O_XX + KC * S
O_TMP = O_XM + 4 * KC * S
O_OH = O_TMP + 4 * S
O_REL = O_OH + 3 * 384
O_E = O_REL + 48
assert O_E + 384 <= TOTAL
O_CM = O_C1
N_CM = C_OH - C_STRICT
O_LW = O_CM + N_CM
O_AR = O_LW + 2 * 4 * P
O_BT = O_AR + 2 * 2 * S
O_KT = O_BT + 2 * S
O_BN = O_KT + 2 * S
O_SW = O_BN + 2 * S
O_SA = O_SW + S
O_CS = O_SA + S
O_CC = O_CS + S
O_EP = O_CC + S
O_EM = O_EP + NCH * (CH + 1)
O_Q1 = O_EM + S
O_RN = O_Q1 + S
O_KK = O_RN + S
O_KS = O_KK + S
O_BTOK = O_KS + S
O_KTOK = O_BTOK + S
O_VTOK = O_KTOK + S
O_AMV = O_VTOK + S
O_U = O_AMV + 2 * S
UB, UR, UK, UKR, UT, UU, UX = range(7)
O_R2 = O_U + 2 * 7 * S
O_GT = O_R2 + S
O_HB = O_GT + NCH * P
O_SB = O_HB + NCH * P
O_Y = O_SB + NCH * P
O_YC = O_Y + S
O_RS = O_YC + S
O_NT0 = O_U
assert O_RS + S <= TOTAL and O_NT0 >= O_B + 2 * KC * S
O_NT1 = O_A
O_FT = O_A + 6 * S
O_XG = O_B
O_HD = O_XG + 2 * KC * S
assert O_HD + 2 * FC * S <= TOTAL
O_QR = O_A + 6 * S
O_QS = O_QR + 2 * S
O_QQ = O_QS + S
O_VR = O_QQ + S
O_BIAS = O_VR + S
O_OA = O_BIAS + 2 * S
O_DF = O_OA + S
O_DW = O_DF + S
assert O_DW + S <= O_B
O_O = O_HD
O_QN = O_O + 2 * KC * S
O_VT = O_QN + 12 * S
O_P = O_VT + 6 * S
O_PT = O_P + 8 * S
N_PT = 3
assert O_PT + N_PT * S <= TOTAL
F_CUTS = (0, O_A, O_C1, O_EP, O_VTOK, TOTAL)
R_CUTS = (0, O_A, O_C1, O_HD + 4 * S, O_HD + 37 * S, TOTAL)


def trunk(nc, xT, stream, lora_out, pvec, const, rel33, out):
    with ExitStack() as ctx:
        def windows(dtype, name, cuts):
            seen = []
            for at, end in zip(cuts, cuts[1:]):
                with ExitStack() as placed:
                    if at:
                        placed.enter_context(nc.sbuf_tensor(f"before_{name}{at}", [P, at], dtype))
                    seen.append((at, end, placed.enter_context(nc.sbuf_tensor(f"{name}{at}", [P, end - at], dtype))))
            return seen

        def window(seen, off, n, lo, hi):
            for at, end, tensor in seen:
                if at <= off < end:
                    return tensor[lo:hi, off - at:off - at + n]

        as_f32, as_f32r = windows(F32, "f", F_CUTS), windows(F32R, "r", R_CUTS)
        ctx.enter_context(nc.sbuf_tensor("whole_map", [P, TOTAL], F32))
        banks = [ctx.enter_context(nc.psum_tensor(f"bank{i}", [P, 512], F32)) for i in range(8)]
        bias_rows = nc.dram_tensor("bias_rows", [3 * 16 * 384], F32, kind="Internal").ap()
        bias_copies = nc.dram_tensor("bias_copies", [3 * 16 * P * 384], F32, kind="Internal").ap()

        class Signals(dict):
            def __missing__(self, name):
                self[name] = ctx.enter_context(nc.semaphore(name))
                return self[name]

        s = Signals()

        def f(off, n=S, lo=0, hi=P):
            return window(as_f32, off, n, lo, hi)

        def r(off, n=S, lo=0, hi=P):
            return window(as_f32r, off, n, lo, hi)

        def rf(off, n=S, lo=0, hi=P):
            return r(off, n, lo, hi).bitcast(F32)

        def con(c, n=P, lo=0, hi=P):
            return f(O_CON + c, n, lo, hi)

        def vec(name, k, lo=0, hi=P):
            return f(O_PV + VECS.index(name) * KC + k, 1, lo, hi)

        def kol(c, lo=0, hi=P):
            return f(O_PV + c, 1, lo, hi)

        def xk(k):
            return f(O_X + k * S)

        def hk(k, shift=0):
            return f(O_H + k * (S + 1) + 1 - shift)

        NORM_SUM = banks[7]
        MIX_ORDER = [0, 3, 1, 4, 2, 5]
        MIX_END = [PAN_W, PAN_K, PAN_A, PAN_V, PAN_G, PAN_WO0]
        NORM_TMP = [O_NT0, O_NT1, O_NT1]
        T_WO0, T_IN0 = PAN_WO0, PAN_WO0 + KC
        T_OUT0 = T_IN0 + 2 * FC
        T_QKV = T_OUT0 + KC
        T_WO1 = T_QKV + 9 * NHP
        T_IN1 = T_WO1 + KC
        T_OUT1 = T_IN1 + 2 * FC

        TILE_AT, PANEL_AT, steps = [], [], 0
        for chunks, tiles in ((KC, T_OUT0), (FC, KC), (KC, T_OUT1 - T_QKV), (FC, KC)):
            for n in range(chunks * tiles):
                if n % 8 == 7 or n % chunks == chunks - 1:
                    steps += 1
                if n % 8 == 7:
                    PANEL_AT.append(steps)
                if n % chunks == chunks - 1:
                    TILE_AT.append(steps)
        assert len(PANEL_AT) == N_PAN

        PREPARE = {0: ["w", "kk", "v_tr", "b_tr"], 1: ["a", "bonus", "a_tr", "k_tr"]}
        FINISH = {0: ["mean", "g"], 1: ["var"]}
        EVEN = ["b", "k", "akv"] + [x + str(n) for n in range(1, N_LEV) for x in "xu"] + ["gh", "r2"]
        ODD = ["b", "k", "x0"] + [f"t{n}" for n in range(1, N_LEV - 1)] + ["pq", "gh"]
        USE = {2: EVEN, 3: ODD, 4: EVEN, 5: ODD, 6: ["y"], 7: [f"s{c}" for c in range(1, NCH - 1)]}

        def bank_turn(b, name, hp):
            if b > 1:
                return USE[b].index(name) + len(USE[b]) * hp
            per = len(PREPARE[b]) + len(FINISH[b])
            if name in PREPARE[b]:
                return PREPARE[b].index(name) + (len(PREPARE[b]) + (hp - 1) * per if hp else 0)
            return FINISH[b].index(name) + (hp + 1) * per - (0 if hp < NHP - 1 else len(PREPARE[b])) \
                + len(PREPARE[b]) - len(FINISH[b])

        def read_out(eng, b, name, hp):
            eng.wait_ge(s[f"bank{b}_free"], bank_turn(b, name, hp) + 1)

        def projected(eng):
            for b in range(2):
                eng.wait_ge(s[f"tile_free{b}"], PAN_WO0 // 2)

        GROUPS = [[("A", 0, 1), ("A", 1, 0), ("A", 1, 1), ("A", 2, 0)], [("A", 2, 1), ("A", 3, 0), ("A", 3, 1)],
                  [("B", 0, 0), ("B", 0, 1), ("B", 1, 0), ("B", 1, 1)],
                  [("B", 2, 0), ("B", 2, 1), ("B", 3, 0), ("B", 3, 1)]]

        def att_turn(b, name, hp):
            return len(USE[b]) * NHP + att_step(b, name, hp)

        def att_step(b, name, hp):
            if b in (2, 3):
                return 4 * hp + 2 * name[0] + name[1] // 2
            if b == 5:
                return 8 * hp + 4 * name[0] + name[1]
            if b in (6, 7):
                return hp
            base = lambda it: 8 + 10 * (it - 1) if it else 0
            if name == "lse":
                return base(hp + 1) + (8 if hp < NHP - 1 else 1)
            if name == 8:
                return base(hp + 1)
            return base(hp) + (name + 1 + (name == 7) if hp else name)

        def att_read(eng, b, name, hp):
            eng.wait_ge(s[f"bank{b}_free"], att_turn(b, name, hp) + 1)

        NORM_ACC = [O_TMP + 2 * S] + [x + 5 * S for x in NORM_TMP]

        def p_of(t):
            if t < T_OUT0:
                return t
            if t < T_QKV:
                return PAN_OUT0 + (FC * (t - T_OUT0 + 1) - 1) // 8
            if t < T_OUT1:
                return PAN_QKV + t - T_QKV
            return PAN_OUT1 + (FC * (t - T_OUT1 + 1) - 1) // 8


        def full(eng, t):
            eng.wait_ge(s["dense"], TILE_AT[t])

        def freed(t):
            return s[f"tile_free{t % 2}"]

        block = ctx.enter_context(nc.Block())

        @block.sync
        def _(sp):
            for k in range(KC):
                sp.dma_start(hk(k), xT[k * P:(k + 1) * P, :]).then_inc(s[f"x_in{k}"], 16)
                if k == 0:
                    sp.dma_start(f(O_CON, 512), const[:, 0:512]).then_inc(s["con_in"], 16)
                    sp.dma_start(f(O_PV, N_PV), pvec).then_inc(s["con_in"], 16)
            sp.dma_start(f(O_OH, 3 * 384, 0, 33), const[0:33, C_OH:C_OH + 3 * 384]).then_inc(s["oh_in"], 16)
            sp.dma_start(f(O_REL, 48, 0, 33), rel33).then_inc(s["oh_in"], 16)

            def panel(p):
                if p >= RAW:
                    sp.wait_ge(s["w_lo"], p - RAW + 1)
                sp.dma_start(f(O_RAW + p % RAW * 1024, 1024), stream[p]).then_inc(s[f"w_raw{p % RAW}"], 16)

            for p in range(PAN_WO0 + RAW):
                panel(p)
            for hp in range(NHP):
                if hp == 0:
                    full(sp, PAN_WO0 - 1)
                    sp.dma_start(f(O_CM, N_CM), const[:, C_STRICT:C_OH]).then_inc(s["mask_in"], 16)
                if hp >= 2:
                    sp.wait_ge(s["g_ps"], hp - 1)
                sp.dma_start(f(O_LW + hp % 2 * 4 * P, 4 * P).rearrange("p (l n) -> p l n", l=4),
                             lora_out[:, :, hp * P:(hp + 1) * P]).then_inc(s[f"lw_in{hp % 2}"], 16)
                if hp == 1:
                    sp.wait_ge(s["bias_dma"], 48)
                    for g in range(3):
                        rows = bias_rows[g * 16 * 384:(g + 1) * 16 * 384]
                        copies = bias_copies[g * 16 * P * 384:(g + 1) * 16 * P * 384]
                        sp.dma_start(copies.rearrange("(h i u) -> h i u", h=16, i=P),
                                     bass.AP(tensor=rows.tensor, offset=g * 16 * 384, ap=[[384, 16], [0, P], [1, 384]]))\
                            .then_inc(s["bias_rep"], 16)
            read_out(sp, 1, "bonus", NHP - 1)
            sp.wait_ge(s["v_tr"], NHP)
            for k in range(KC):
                sp.dma_start(xk(k), xT[k * P:(k + 1) * P, :]).then_inc(s["x_again"], 16)
            for p in range(PAN_WO0 + RAW, N_PAN):
                panel(p)
                hp, i = divmod(p - PAN_QKV, 9)
                if 0 <= hp < NHP and i in (5, 8):
                    h = 0 if i == 5 else 1
                    if hp == 0 and h == 0:
                        sp.wait_ge(s["bias_rep"], 48)
                        sp.wait_ge(s["hd_lo"], FC)
                        full(sp, T_QKV - 1)
                    if hp:
                        att_read(sp, 3, (h, 3), hp - 1)
                    for g, at, width in ((0, 0, 2 * P), (1, 2 * P, P), (2, 3 * P, P)):
                        src = bass.AP(tensor=bias_copies.tensor, offset=(g * 16 + 2 * hp + h) * P * 384 + P - 1,
                                      ap=[[383, P], [1, width]])
                        sp.dma_start(f(O_BIAS + h * S + at, width), src).then_inc(s[f"bias_in{h}"], 16)
            out_k = out.rearrange("(k p) t -> k p t", p=P)
            for m in range(KC):
                sp.wait_ge(freed(T_OUT1 + m), (T_OUT1 + m) // 2 + 1)
                sp.dma_start(out_k[m], xk(m)).then_inc(s["out_done"], 16)
            sp.wait_ge(s["out_done"], 16 * KC)


        @block.tensor
        def _(pe):
            def mm(out, lhsT, rhs, start=True, stop=True):
                return nc.tensor.matmul(out, lhsT, rhs, start=start, stop=stop, skip_group_check=True)

            def flip(out, in_):
                return nc.tensor.transpose(out, in_, con(C_ID))

            def product(t, q0, rhs_hi, rhs_lo, chunks, gate=None, gate0=0):
                if t >= 2:
                    pe.wait_ge(freed(t), t // 2)
                bank = banks[t % 2]
                for j in range(chunks):
                    p, col = divmod(q0 + j, 8)
                    if j == 0 or col == 0:
                        pe.wait_ge(s["w_lo"], p + 1)
                    if gate:
                        pe.wait_ge(s[gate], gate0 + j + 1)
                    w_hi = r(O_WHI + p % PAN * 1024 + col * P, P)
                    w_lo = r(O_WLO + p % PAN * 1024 + col * P, P)
                    mm(bank[:, :], w_hi, rhs_hi(j), j == 0, False)
                    mm(bank[:, :], w_hi, rhs_lo(j), False, False)
                    last = mm(bank[:, :], w_lo, rhs_hi(j), False, j == chunks - 1)
                    if col == 7 or j == chunks - 1:
                        last.then_inc(s["dense"], 1)

            def norm_sum(n):
                pe.wait_ge(s["sq_sum"], KC * (n + 1))
                if n:
                    pe.wait_ge(s["ln_norm"], n)
                mm(NORM_SUM[:, :], con(C_ONES), f(NORM_ACC[n])).then_inc(s["norm_ps"], 1)

            pe.wait_ge(s["con_in"], 32)
            norm_sum(0)
            t = 0
            for j in range(6):
                b = O_XM + j % 2 * 2 * KC * S
                first = t
                while t < MIX_END[j]:
                    product(t, 8 * t, lambda c, b=b: r(b + c * S), lambda c, b=b: r(b + (KC + c) * S), KC,
                            "mix_lo" if t == first else None, KC * j)
                    t += 1
            pe.wait_ge(s["oh_in"], 32)
            for g in range(3):
                if g:
                    pe.wait_ge(s["bias_sb"], g)
                mm(banks[6][0:16, 0:384], f(O_REL + 16 * g, 16, 0, 33),
                   f(O_OH + 384 * g, 384, 0, 33)).then_inc(s["bias_ps"], 1)

            def fill(b, name, hp, n=1):
                c = bank_turn(b, name, hp)
                if c:
                    pe.wait_ge(s[f"bank{b}_free"], c)

            def prepare_gates(hp):
                lw = O_LW + hp % 2 * 4 * P
                pe.wait_ge(s[f"lw_in{hp % 2}"], 16 * (hp // 2 + 1))
                fill(0, "w", hp)
                mm(banks[0][:, :], f(lw, P, 0, LORA), f(O_TW, S, 0, LORA)).then_inc(s["w_ps"], 1)
                fill(1, "a", hp)
                mm(banks[1][:, :], f(lw + P, P, 0, LORA), f(O_TA, S, 0, LORA)).then_inc(s["a_ps"], 1)

            def prepare_sums(hp):
                fill(0, "kk", hp)
                pe.wait_ge(s["kk_sq"], hp + 1)
                mm(banks[0][:, :], con(C_HEAD), f(O_Q1)).then_inc(s["kk_ps"], 1)
                fill(1, "bonus", hp)
                pe.wait_ge(s["rk"], hp + 1)
                mm(banks[1][:, :], con(C_HEAD), f(O_Q1)).then_inc(s["bonus_ps"], 1)

            def prepare_token_major(hp):
                a = hp % 2
                fill(0, "v_tr", hp)
                for q in range(NT):
                    last = flip(banks[0][:, q * P:(q + 1) * P], f(O_X + hp * S + q * P, P))
                last.then_inc(s["v_tr"], 1)
                fill(1, "a_tr", hp)
                pe.wait_ge(s["ar_a"], hp + 1)
                for q in range(NT):
                    last = flip(banks[1][:, q * P:(q + 1) * P], f(O_AR + a * 2 * S + q * 2 * P, P))
                last.then_inc(s["a_tr"], 1)
                fill(0, "b_tr", hp)
                pe.wait_ge(s["bt"], hp + 1)
                for q in range(NT):
                    last = flip(banks[0][:, q * P:(q + 1) * P], f(O_BT + a * S + q * P, P))
                last.then_inc(s["b_tr"], 1)
                fill(1, "k_tr", hp)
                pe.wait_ge(s["kt"], hp + 1)
                for q in range(NT):
                    last = flip(banks[1][:, q * P:(q + 1) * P], f(O_KT + a * S + q * P, P))
                last.then_inc(s["k_tr"], 1)

            def scores(hp, h, kind):
                a, lo = hp % 2, HD * h
                src = (O_BT if kind == "b" else O_KT) + a * S
                pe.wait_ge(s["ar_r"], hp + 1)
                pe.wait_ge(s["bt" if kind == "b" else "kt"], hp + 1)
                for half in range(2):
                    b = 2 + 2 * h + half
                    fill(b, kind, hp)
                    for q in (2 * half, 2 * half + 1):
                        last = mm(banks[b][:, q % 2 * 2 * P:(q % 2 + 1) * 2 * P], f(src + q * P, P, lo, lo + HD),
                                  f(O_AR + a * 2 * S + q * 2 * P, 2 * P, lo, lo + HD))
                    last.then_inc(s[f"{kind}_sc{h}"], 1)

            def u(h, n, q=0, w=S):
                return f(O_U + (h * 7 + n) * S + q * P, w)

            def amv(h, q):
                return O_AMV + h * S + q * P

            def a_k_v(hp, h):
                b = 2 + 2 * h
                fill(b, "akv", hp)
                read_out(pe, 2 + 2 * h, "k", hp)
                read_out(pe, 3 + 2 * h, "k", hp)
                read_out(pe, 0, "v_tr", hp)
                for q in range(NT):
                    last = mm(banks[b][:, q * HD:(q + 1) * HD], u(h, UK, q, P), f(O_VTOK + q * P + h * HD, HD))
                last.then_inc(s[f"akv_ps{h}"], 1)

            def inverse(hp, h, n):
                b = 2 + 2 * h
                if n == 0:
                    fill(b + 1, "x0", hp)
                    pe.wait_ge(s[f"bi{h}"], hp + 1)
                    for q in range(NT):
                        last = mm(banks[b + 1][:, q * P:(q + 1) * P], u(h, UB, q, P), con(C_ID))
                    last.then_inc(s[f"x_ps{h}"], 1)
                    return
                fill(b, f"x{n}", hp)
                read_out(pe, b + 1, f"t{n - 1}" if n > 1 else "x0", hp)
                for q in range(NT):
                    last = mm(banks[b][:, q * P:(q + 1) * P], u(h, UB, q, P), u(h, UT, q, P))
                last.then_inc(s[f"x_ps{h}"], 1)

            def inverse_update(hp, h, n):
                b = 2 + 2 * h
                read_out(pe, b, f"x{n}", hp)
                if n == 1:
                    pe.wait_ge(s[f"u0_{h}"], hp + 1)
                if n < N_LEV - 1:
                    fill(b + 1, f"t{n}", hp)
                    for q in range(NT):
                        last = mm(banks[b + 1][:, q * P:(q + 1) * P], u(h, UU, q, P), u(h, UX, q, P))
                    last.then_inc(s[f"t_ps{h}"], 1)
                fill(b, f"u{n}", hp)
                for q in range(NT):
                    last = mm(banks[b][:, q * P:(q + 1) * P], u(h, UX, q, P), u(h, UU, q, P))
                last.then_inc(s[f"u_ps{h}"], 1)

            def solve(hp, h):
                b = 3 + 2 * h
                fill(b, "pq", hp)
                read_out(pe, b - 1, f"u{N_LEV - 1}", hp)
                read_out(pe, b - 1, "akv", hp)
                read_out(pe, 1, "a_tr", hp)
                for q in range(NT):
                    last = mm(banks[b][:, q * P:(q + 1) * P], u(h, UU, q, P), f(amv(h, q), P))
                last.then_inc(s[f"pq_ps{h}"], 1)

            def transitions(hp, h):
                lo = HD * h
                read_out(pe, 3 + 2 * h, "pq", hp)
                read_out(pe, 0, "b_tr", hp)
                read_out(pe, 1, "k_tr", hp)
                for e in range(2):
                    b = 2 + 2 * h + e
                    fill(b, "gh", hp)
                    el, eh = CH * e, CH * (e + 1)
                    for q in range(NT):
                        pq = O_U + (h * 7 + UK) * S + q * P
                        btok = f(O_BTOK + q * P + lo, HD, el, eh)
                        o = banks[b][lo:lo + HD, q * P:(q + 1) * P]
                        mm(o[:, 0:HD], f(pq, HD, el, eh), btok, q == 0, False)
                        mm(o[:, HD:P], btok, f(pq + HD, HD, el, eh), False, False)
                        last = mm(o[:, HD:P], f(O_KTOK + q * P + lo, HD, el, eh),
                                  f(O_VTOK + q * P + lo, HD, el, eh), False, True)
                    last.then_inc(s[f"gh_ps{h}"], 1)

            def readout(hp, h):
                lo = HD * h
                b = 2 + 2 * h
                fill(b, "r2", hp)
                for q in range(NT):
                    pq = O_U + (h * 7 + UK) * S + q * P
                    last = mm(banks[b][lo:lo + HD, q * P:(q + 1) * P], f(pq, HD), u(h, UR, q, P))
                last.then_inc(s[f"r2_ps{h}"], 1)
                if h == 0:
                    pe.wait_ge(s["bias_sb"], 3)
                    fill(6, "y", hp)
                for q in range(NT):
                    pq = O_U + (h * 7 + UK) * S + q * P
                    o = banks[6][lo:lo + HD, q * P:(q + 1) * P]
                    mm(o, f(pq + HD, HD), u(h, UR, q, P), q == 0, False)
                    last = mm(o, f(O_VTOK + q * P + lo, HD), u(h, UKR, q, P), False, False)
                last.then_inc(s[f"y0_ps{h}"], 1)

            def walk(hp, c):
                state = f(O_SB + c * P, P) if c > 1 else f(O_HB, P)
                if c == 1:
                    for b in (2, 3, 4, 5):
                        read_out(pe, b, "gh", hp)
                    for b in (2, 4):
                        read_out(pe, b, "r2", hp)
                else:
                    read_out(pe, 7, f"s{c - 1}", hp)
                if c < NCH - 1:
                    fill(7, f"s{c}", hp)
                    mm(banks[7][:, 0:P], f(O_GT + c * P, P), state).then_inc(s["s_ps"], 1)
                last = mm(banks[6][:, c * CH:(c + 1) * CH], state, f(O_R2 + c * CH, CH), False, c == NCH - 1)
                if c == NCH - 1:
                    last.then_inc(s["y_ps"], 1)

            def finish(hp, part):
                if part == 0:
                    fill(0, "mean", hp)
                    read_out(pe, 6, "y", hp)
                    mm(banks[0][:, :], con(C_MEAN), f(O_Y)).then_inc(s["mean_ps"], 1)
                elif part == 1:
                    fill(1, "var", hp)
                    pe.wait_ge(s["y_sq"], hp + 1)
                    mm(banks[1][:, :], con(C_MEAN), f(O_Y)).then_inc(s["var_ps"], 1)
                else:
                    fill(0, "g", hp)
                    lw = O_LW + hp % 2 * 4 * P + 2 * P
                    mm(banks[0][:, :], f(lw, P), f(O_TG), True, False)
                    mm(banks[0][:, :], f(lw + P, P, 0, GLORA - P), f(O_TG + S, S, 0, GLORA - P),
                       False, True).then_inc(s["g_ps"], 1)

            projected(pe)
            prepare_gates(0)
            prepare_sums(0)
            prepare_token_major(0)
            for hp in range(NHP):
                for h in range(2):
                    scores(hp, h, "b")
                if hp < NHP - 1:
                    prepare_gates(hp + 1)
                for h in range(2):
                    scores(hp, h, "k")
                for h in range(2):
                    a_k_v(hp, h)
                for n in range(N_LEV):
                    for h in range(2):
                        inverse(hp, h, n)
                    if n:
                        for h in range(2):
                            inverse_update(hp, h, n)
                    if n == 3 and hp < NHP - 1:
                        prepare_sums(hp + 1)
                for h in range(2):
                    solve(hp, h)
                for h in range(2):
                    transitions(hp, h)
                for h in range(2):
                    readout(hp, h)
                if hp < NHP - 1:
                    prepare_token_major(hp + 1)
                for c in range(1, NCH):
                    walk(hp, c)
                for part in range(3):
                    finish(hp, part)

            for b in range(2):
                pe.wait_ge(s[f"bank{b}_free"], bank_turn(b, "g" if b == 0 else "var", NHP - 1) + 1)
            for m in range(KC):
                product(T_WO0 + m, 8 * (PAN_WO0 + m), lambda c: r(O_A + c * S), lambda c: r(O_A + (KC + c) * S),
                        KC, "yo_lo" if m == 0 else None)
            norm_sum(1)

            def feed_forward(n, t_in, pan_in, t_out, pan_out, norm_next):
                for i in range(2 * FC):
                    product(t_in + i, 8 * (pan_in + i), lambda c: r(O_XG + c * S), lambda c: r(O_XG + (KC + c) * S),
                            KC, "xg_lo" if i == 0 else None, KC * (2 * n))
                for m in range(KC):
                    product(t_out + m, 8 * pan_out + FC * m, lambda c: r(O_HD + c * S),
                            lambda c: r(O_HD + (FC + c) * S), FC, "hd_lo" if m == 0 else None, FC * n)
                if norm_next:
                    norm_sum(norm_next)

            feed_forward(0, T_IN0, PAN_IN0, T_OUT0, PAN_OUT0, 2)

            def qkv(hp, g, kind):
                return O_QN + (hp % 2 * 6 + g * 2 + kind) * S

            def fill_att(b, name, hp):
                pe.wait_ge(s[f"bank{b}_free"], att_turn(b, name, hp))

            def projection_aux(hp, i):
                g, kind = divmod(i, 3)
                fill_att(4, i, hp)
                if kind < 2:
                    pe.wait_ge(s["q_sq"], 6 * hp + 2 * g + kind + 1)
                    mm(banks[4][:, :], con(C_HEAD), f(O_QQ)).then_inc(s["aux_ps"], 1)
                else:
                    pe.wait_ge(freed(T_QKV + 9 * hp + i), (T_QKV + 9 * hp + i) // 2 + 1)
                    for q in range(NT):
                        last = flip(banks[4][:, q * P:(q + 1) * P], f(O_VR + q * P, P))
                    last.then_inc(s["aux_ps"], 1)

            def logits(hp, h, pair):
                lo, b = HD * h, 2 + pair % 2
                fill_att(b, (h, pair), hp)
                pe.wait_ge(s["qk_norm"], 6 * hp + (2 if pair < 2 else 6))
                for e in range(2):
                    n = pair % 2 * 2 + e
                    o = banks[b][:, e * 2 * P:(e + 1) * 2 * P]
                    if pair < 2:
                        first = P if n == 0 else 0
                        last = mm(o[:, first:2 * P], f(qkv(hp, 0, 0) + n * P, P, lo, lo + HD),
                                  f(qkv(hp, 0, 1) + (n - 1) * P + first, 2 * P - first, lo, lo + HD))
                    else:
                        for g in (1, 2):
                            last = mm(o[:, (g - 1) * P:g * P], f(qkv(hp, g, 0) + n * P, P, lo, lo + HD),
                                      f(qkv(hp, g, 1) + n * P, P, lo, lo + HD))
                last.then_inc(s[f"logits{b}"], 1)

            def block_of(h, what):
                kind, n, e = what
                return O_P + h * 4 * S + (n + (4 if kind == "B" else 0)) * 2 * P + e * P

            def flip_probs(hp, h, g):
                fill_att(5, (h, g), hp)
                pe.wait_ge(s[f"probs{h}"], 8 * hp + (4 if g < 2 else 8))
                for j, what in enumerate(GROUPS[g]):
                    last = flip(banks[5][:, j * P:(j + 1) * P], f(block_of(h, what), P))
                last.then_inc(s["flipped"], 1)

            def attend(hp, h, g):
                lo, n = HD * h, 8 * hp + 4 * h + g
                att_read(pe, 5, (h, g), hp)
                if h == 0 and g in (0, 2):
                    fill_att(6 if g == 0 else 7, None, hp)
                if g == 2:
                    att_read(pe, 4, 8, hp)
                if g == 0:
                    att_read(pe, 4, 2, hp)
                for j, (kind, q, e) in enumerate(GROUPS[g]):
                    if kind == "A":
                        b, v = 6, O_VT + hp % 2 * 3 * S + (q - 1 + e) * P
                    else:
                        b, v = 7, O_VT + (hp % 2 * 3 + 1 + e) * S + q * P
                    last = mm(banks[b][lo:lo + HD, q * P:(q + 1) * P], f(v + lo, HD),
                              f(O_PT + n % N_PT * S + j * P, P), g in (0, 2) and j == 0, False)
                last.then_inc(s["attended"], 1)

            def lse_difference(hp):
                fill_att(4, "lse", hp)
                for h in range(2):
                    pe.wait_ge(s[f"lse{h}"], 2 * (hp + 1))
                    lo = HD * h
                    for n in range(2 * NT):
                        o = banks[4][lo:lo + HD, n * P:(n + 1) * P] if n < NT else \
                            banks[4][lo:lo + HD, n - NT:S:4]
                        last = mm(o, bc(f(O_SM + 40 * h + 32 + n, 1), (0, HD)), con(C_ID), n == 0, False)
                last.then_inc(s["lse_ps"], 1)

            for it in range(NHP + 1):
                a = it - 1
                for i in range(9):
                    if it < NHP:
                        t = T_QKV + 9 * it + i
                        product(t, 8 * (PAN_QKV + 9 * it + i), lambda c: r(O_XG + c * S),
                                lambda c: r(O_XG + (KC + c) * S), KC, "xg_lo" if it == i == 0 else None, KC)
                    if i and it < NHP:
                        projection_aux(it, i - 1)
                    if a < 0:
                        continue
                    if i == 0:
                        projection_aux(a, 8)
                    if i < 4:
                        logits(a, i // 2, i % 2 * 2)
                        logits(a, i // 2, i % 2 * 2 + 1)
                    for h, g in {3: [(0, 0)], 4: [(0, 1)], 5: [(0, 2)], 6: [(0, 3), (1, 0)], 7: [(1, 1)],
                                 8: [(1, 2)]}.get(i, []):
                        attend(a, h, g)
                    if i == 7:
                        lse_difference(a)
                    for h, g in {2: [(0, 0)], 3: [(0, 1)], 4: [(0, 2)], 5: [(0, 3), (1, 0)], 6: [(1, 1)],
                                 7: [(1, 2)], 8: [(1, 3)]}.get(i, []):
                        flip_probs(a, h, g)
                    if i == 8:
                        attend(a, 1, 3)
            att_read(pe, 7, None, NHP - 1)
            for m in range(KC):
                product(T_WO1 + m, 8 * (PAN_WO1 + m), lambda c: r(O_O + c * S), lambda c: r(O_O + (KC + c) * S),
                        KC, "att_lo" if m == 0 else None)
            norm_sum(3)
            feed_forward(1, T_IN1, PAN_IN1, T_OUT1, PAN_OUT1, None)


        @block.scalar
        def _(act):
            A = nc.scalar.activation
            ahead = [0]

            def split_high(panel):
                while ahead[0] <= min(panel, N_PAN - 1):
                    p = ahead[0]
                    act.wait_ge(s[f"w_raw{p % RAW}"], 16 * (p // RAW + 1))
                    if p >= PAN:
                        act.wait_ge(s["dense"], PANEL_AT[p - PAN])
                    A(r(O_WHI + p % PAN * 1024, 1024), f(O_RAW + p % RAW * 1024, 1024), ACT.Copy)\
                        .then_inc(s["w_hi"], 1)
                    ahead[0] += 1

            def rsqrt_norm(n):
                act.wait_ge(s["norm_ps"], n + 1)
                A(f(O_RSTD), NORM_SUM[:, :], ACT.Ln, bias=kol(K_EPS), scale=1.0 / D).then_inc(s["ln_norm"], 1)
                act.wait_ge(s["ln_norm"], n + 1)
                A(f(O_RSTD), f(O_RSTD), ACT.Exp, scale=-0.5).then_inc(s["rstd"], 1)

            for k in range(KC):
                act.wait_ge(s[f"x_in{k}"], 16)
                if k >= 2:
                    act.wait_ge(s["sq_sum"], k - 1)
                A(f(O_TMP + k % 2 * S), hk(k), ACT.Square).then_inc(s["sq"], 1)
            act.wait_ge(s["con_in"], 32)
            rsqrt_norm(0)
            split_high(LEAD)
            OUT = {PAN_R + k: (O_A + k * S, ACT.Copy) for k in range(KC)}
            OUT.update({PAN_K + k: (O_A + (KC + k) * S, ACT.Copy) for k in range(KC)})
            OUT.update({PAN_V + k: (O_X + k * S, ACT.Copy) for k in range(KC)})
            OUT.update({PAN_W: (O_TW, ACT.Tanh), PAN_A: (O_TA, ACT.Copy),
                        PAN_G: (O_TG, ACT.Sigmoid), PAN_G + 1: (O_TG + S, ACT.Sigmoid)})

            def take_projections(first, last):
                for t in range(first, last):
                    split_high(t + LEAD)
                    full(act, t)
                    off, func = OUT[t]
                    A(f(off), banks[t % 2][:, :], func).then_inc(freed(t), 1)

            for j in range(8):
                if j >= 2:
                    take_projections(MIX_END[j - 3] if j > 2 else 0, MIX_END[j - 2])
                if j < 6:
                    for k in range(KC):
                        i = KC * j + k
                        act.wait_ge(s["mix_t"], i + 1)
                        A(r(O_XM + (j % 2 * 2 * KC + k) * S), f(O_TMP + i % 4 * S), ACT.Copy)\
                            .then_inc(s["mix_hi"], 1)
            for g in range(3):
                act.wait_ge(s["bias_ps"], g + 1)
                if g:
                    act.wait_ge(s["bias_dma"], 16 * g)
                A(f(O_E, 384, 0, 16), banks[6][0:16, 0:384], ACT.Copy).then_inc(s["bias_sb"], 1)
                act.wait_ge(s["bias_sb"], g + 1)
                rows = bias_rows[g * 16 * 384:(g + 1) * 16 * 384].rearrange("(h u) -> h u", h=16)
                act.dma_start(rows, f(O_E, 384, 0, 16)).then_inc(s["bias_dma"], 16)
            act.wait_ge(s["bias_dma"], 48)

            def take(b, name, hp, ready, out, func=ACT.Copy, in_=None, **kw):
                act.wait_ge(*ready)
                return A(out, banks[b][:, :] if in_ is None else in_, func, **kw).then_inc(s[f"bank{b}_free"], 1)

            def gates(hp):
                if hp:
                    act.wait_ge(s["bt"], hp)
                take(0, "w", hp, (s["w_ps"], hp + 1), f(O_SW), ACT.Sigmoid, bias=vec("w0", hp))
                take(1, "a", hp, (s["a_ps"], hp + 1), f(O_SA), ACT.Sigmoid, bias=vec("a0", hp))

            def decays(hp):
                act.wait_ge(s["cc"], hp + 1)
                ep = f(O_EP, NCH * (CH + 1))
                mid = bc(f(O_CS + CH // 2 - 1), (CH, NCH), (1, 1))
                A(bc(ep, (CH + 1, NCH), (1, 1)), mid, ACT.Exp, scale=KAPPA)
                A(bc(f(O_EP + 1, NCH * (CH + 1) - 1), (CH + 1, NCH), (1, CH)), bc(f(O_CC), (CH, NCH), (1, CH)),
                  ACT.Exp, scale=-KAPPA)
                A(bc(f(O_SM, NCH), (1, NCH), (1, 1)), mid, ACT.Exp, scale=-KAPPA).then_inc(s["ep"], 1)
                A(f(O_EM), f(O_CC), ACT.Exp, scale=KAPPA).then_inc(s["em"], 1)

            def key_norm(hp):
                if hp:
                    act.wait_ge(s["bonus_ps"], hp)
                A(f(O_Q1), f(O_A + (KC + hp) * S), ACT.Square, scale=vec("k_k", hp)).then_inc(s["kk_sq"], 1)
                read_out(act, 0, "kk", hp)
                A(f(O_RN), f(O_RN), ACT.Ln, scale=65536.0).then_inc(s["kk_ln"], 1)
                act.wait_ge(s["kk_ln"], hp + 1)
                A(f(O_RN), f(O_RN), ACT.Exp, scale=-0.5, bias=kol(K_KKB)).then_inc(s["kk_rs"], 1)

            def token_major(hp):
                take(0, "v_tr", hp, (s["v_tr"], hp + 1), f(O_VTOK))
                take(1, "a_tr", hp, (s["a_tr"], hp + 1),
                     bc(f(O_AMV, 2 * S), (S, 2), (P, NT), (1, HD)),
                     in_=banks[1][:, :].rearrange("p (q h n) -> p h q n", q=NT, h=2), scale=-1.0)
                take(0, "b_tr", hp, (s["b_tr"], hp + 1), f(O_BTOK))
                take(1, "k_tr", hp, (s["k_tr"], hp + 1), f(O_KTOK))

            def ub(h, n):
                return f(O_U + (h * 7 + n) * S)

            def finish(hp):
                take(6, "y", hp, (s["y_ps"], hp + 1), f(O_Y))
                read_out(act, 0, "mean", hp)
                A(f(O_Y), f(O_YC), ACT.Square).then_inc(s["y_sq"], 1)
                act.wait_ge(s["var_ps"], hp + 1)
                A(f(O_RS), banks[1][:, :], ACT.Ln, bias=kol(K_LNEPS)).then_inc(s["bank1_free"], 1)
                read_out(act, 1, "var", hp)
                A(f(O_RS), f(O_RS), ACT.Exp, scale=-0.5).then_inc(s["y_rs"], 1)
                read_out(act, 0, "g", hp)
                A(r(O_A + hp * S), f(O_YC), ACT.Copy).then_inc(s["yo_hi"], 1)

            projected(act)
            gates(0)
            decays(0)
            key_norm(0)
            token_major(0)
            for hp in range(NHP):
                if hp < NHP - 1:
                    gates(hp + 1)
                for h in range(2):
                    take(2 + 2 * h, "akv", hp, (s[f"akv_ps{h}"], hp + 1),
                         bc(f(O_AMV + h * S + HD, S - HD), (P, NT), (1, HD)),
                         in_=banks[2 + 2 * h][:, 0:NT * HD].rearrange("p (q n) -> p q n", q=NT))
                for n in range(1, N_LEV):
                    for h in range(2):
                        if n < N_LEV - 1:
                            take(3 + 2 * h, f"t{n}", hp, (s[f"t_ps{h}"], (N_LEV - 2) * hp + n), ub(h, UT))
                        take(2 + 2 * h, f"u{n}", hp, (s[f"u_ps{h}"], (N_LEV - 1) * hp + n), ub(h, UU))
                    if hp < NHP - 1 and n == 2:
                        decays(hp + 1)
                        key_norm(hp + 1)
                for h in range(2):
                    take(3 + 2 * h, "pq", hp, (s[f"pq_ps{h}"], hp + 1), ub(h, UK))
                if hp < NHP - 1:
                    token_major(hp + 1)
                finish(hp)

            def residual(n, t0):
                for m in range(KC):
                    split_high(p_of(t0 + m) + LEAD)
                    i = KC * n + m
                    base = NORM_TMP[n]
                    act.wait_ge(s["xg_t"], i + 1)
                    A(r(O_XG + m * S), f(base + i % 2 * S), ACT.Copy).then_inc(s["xg_hi"], 1)
                    act.wait_ge(s["sq_sum"], KC + i - 1)
                    A(f(base + (2 + i % 2) * S), xk(m), ACT.Square).then_inc(s["sq"], 1)
                rsqrt_norm(n + 1)

            def feed_forward(n, t_in, t_out):
                for i in range(FC):
                    split_high(p_of(t_in + 2 * i) + LEAD)
                    act.wait_ge(freed(t_in + 2 * i), (t_in + 2 * i) // 2 + 1)
                    A(f(O_FT + (2 + i % 2) * S), f(O_FT + i % 2 * S), ACT.Silu).then_inc(s["silu"], 1)
                    split_high(p_of(t_in + 2 * i + 1) + LEAD)
                    act.wait_ge(s["hd"], FC * n + i + 1)
                    A(r(O_HD + i * S), f(O_FT + (6 + i % 2) * S), ACT.Copy).then_inc(s["hd_hi"], 1)

            residual(0, T_WO0)
            feed_forward(0, T_IN0, T_OUT0)
            residual(1, T_OUT0)

            def free(ins, b):
                ins.then_inc(s[f"bank{b}_free"], 1)

            def squares(hp, i):
                g, kind = divmod(i, 3)
                if kind < 2:
                    n, t = 6 * hp + 2 * g + kind, T_QKV + 9 * hp + i
                    act.wait_ge(freed(t), t // 2 + 1)
                    if n:
                        act.wait_ge(s["aux_ps"], n + n // 2 - (1 if n % 2 == 0 else 0))
                    A(f(O_QQ), f(O_QR + n % 2 * S), ACT.Square).then_inc(s["q_sq"], 1)

            def projection_aux(hp, i):
                g, kind = divmod(i, 3)
                act.wait_ge(s["aux_ps"], 9 * hp + i + 1)
                if kind < 2:
                    n = 6 * hp + 2 * g + kind
                    if n:
                        act.wait_ge(s["qk_norm"], n)
                    free(A(f(O_QS), banks[4][:, :], ACT.Ln, bias=kol(K_EPS), scale=1.0 / HD), 4)
                    att_read(act, 4, i, hp)
                    A(f(O_QS), f(O_QS), ACT.Exp, scale=-0.5).then_inc(s["q_rs"], 1)
                else:
                    free(A(f(O_VT + (hp % 2 * 3 + g) * S), banks[4][:, :], ACT.Copy), 4)

            def exps(hp, h, half):
                sm = O_SM + 40 * h
                act.wait_ge(s[f"neg_max{h}"], 2 * hp + half + 1)
                for n in range(4 * half, 4 * half + 4):
                    first = P if n == 0 else 0
                    tile = f(O_P + h * 4 * S + n * 2 * P + first, 2 * P - first)
                    A(tile, tile, ACT.Exp, bias=f(sm + 8 + n, 1), accum_out=f(sm + 16 + n, 1))\
                        .then_inc(s[f"exp{h}"], 1)
                if hp:
                    act.wait_ge(s["lse_ps"], hp)
                act.wait_ge(s[f"exp{h}"], 8 * hp + 4 * half + 4)
                A(f(sm + 32 + 4 * half, 4), f(sm + 16 + 4 * half, 4), ACT.Ln).then_inc(s[f"log{h}"], 1)

            def keep_flipped(hp, h, g):
                n = 8 * hp + 4 * h + g
                act.wait_ge(s["flipped"], n + 1)
                if n >= N_PT:
                    act.wait_ge(s["attended"], n - N_PT + 1)
                w = len(GROUPS[g]) * P
                free(A(f(O_PT + n % N_PT * S, w), banks[5][:, 0:w], ACT.Copy), 5)

            def combine(hp):
                att_read(act, 7, None, hp)
                A(r(O_O + hp * S), f(O_DF), ACT.Copy).then_inc(s["att_hi"], 1)

            for it in range(NHP + 1):
                a = it - 1
                for i in range(9):
                    if it < NHP:
                        split_high(p_of(T_QKV + 9 * it + i) + LEAD)
                        if i:
                            projection_aux(it, i - 1)
                        squares(it, i)
                    if a < 0:
                        continue
                    if i == 0:
                        projection_aux(a, 8)
                        if a:
                            combine(a - 1)
                    if 1 <= i <= 4:
                        exps(a, (i - 1) // 2, (i - 1) % 2)
                    for h, g in {2: [(0, 0)], 3: [(0, 1)], 4: [(0, 2)], 5: [(0, 3), (1, 0)], 6: [(1, 1)],
                                 7: [(1, 2)], 8: [(1, 3)]}.get(i, []):
                        keep_flipped(a, h, g)
                    if i == 7:
                        act.wait_ge(s["lse_ps"], a + 1)
                        if a:
                            act.wait_ge(s["att_lo"], a)
                        free(A(f(O_DW), banks[4][:, :], ACT.Sigmoid), 4)
                    if i == 8:
                        act.wait_ge(s["attended"], 8 * a + 6)
                        if a:
                            act.wait_ge(s["att_lo"], a)
                        free(A(f(O_OA), banks[6][:, :], ACT.Copy), 6)
            combine(NHP - 1)
            residual(2, T_WO1)
            feed_forward(1, T_IN1, T_OUT1)
            for m in range(KC):
                split_high(p_of(T_OUT1 + m) + LEAD)


        @block.vector
        def _(dve):
            V = nc.vector
            TT, STT, TS = V.tensor_tensor, V.scalar_tensor_tensor, V.tensor_scalar
            ahead = [0]

            def split_low(panel):
                while ahead[0] <= min(panel, N_PAN - 1):
                    p = ahead[0]
                    dve.wait_ge(s["w_hi"], p + 1)
                    TT(r(O_WLO + p % PAN * 1024, 1024), f(O_RAW + p % RAW * 1024, 1024),
                       rf(O_WHI + p % PAN * 1024, 1024), ALU.subtract).then_inc(s["w_lo"], 1)
                    ahead[0] += 1

            def add_squares(i, sq, acc, first):
                dve.wait_ge(s["sq"], i + 1)
                if first:
                    V.tensor_copy(f(acc), f(sq)).then_inc(s["sq_sum"], 1)
                else:
                    dve.wait_ge(s["sq_sum"], i)
                    TT(f(acc), f(acc), f(sq), ALU.add).then_inc(s["sq_sum"], 1)

            for k in range(KC):
                V.memset(f(O_H + k * (S + 1), 1), 0.0).then_inc(s["pad"], 1)
            for k in range(KC):
                add_squares(k, O_TMP + k % 2 * S, NORM_ACC[0], k == 0)
            dve.wait_ge(s["rstd"], 1)
            dve.wait_ge(s["con_in"], 32)
            for k in range(KC):
                STT(hk(k), hk(k), vec("mix0", k), f(O_RSTD), ALU.mult, ALU.mult).then_inc(s["h"], 1)
            dve.wait_ge(s["pad"], KC)
            for k in range(KC):
                dve.wait_ge(s["h"], k + 1)
                TT(f(O_XX + k * S), hk(k, 1), hk(k), ALU.subtract).then_inc(s["xx"], 1)
            split_low(LEAD)

            def mix_low(i):
                j, k = divmod(i, KC)
                dve.wait_ge(s["mix_hi"], i + 1)
                at = O_XM + (j % 2 * 2 * KC + k) * S
                TT(r(at + KC * S), f(O_TMP + i % 4 * S), rf(at), ALU.subtract).then_inc(s["mix_lo"], 1)

            for j in range(6):
                if j >= 2:
                    split_low(MIX_END[j - 2] - 1 + LEAD)
                    dve.wait_ge(s["dense"], PANEL_AT[MIX_END[j - 2] - 1])
                for k in range(KC):
                    i = KC * j + k
                    dve.wait_ge(s["xx"], k + 1)
                    if i >= 4:
                        dve.wait_ge(s["mix_lo"], i - 3)
                    STT(f(O_TMP + i % 4 * S), f(O_XX + k * S), vec(f"mu{MIX_ORDER[j]}", k), hk(k),
                        ALU.mult, ALU.add).then_inc(s["mix_t"], 1)
                    if k >= 2:
                        mix_low(i - 2)
                mix_low(KC * j + KC - 2)
                mix_low(KC * j + KC - 1)
            split_low(PAN_WO0 - 1 + LEAD)

            def cen(off, step=CH, width=CH):
                return bc(f(off), (step, NCH), (1, width))

            def free(ins, b):
                return ins.then_inc(s[f"bank{b}_free"], 1)

            def decay_sums(hp):
                read_out(dve, 0, "w", hp)
                if hp:
                    dve.wait_ge(s["em"], hp)
                V.tensor_tensor_scan(f(O_CS), f(O_CM + C_RESET - C_STRICT), f(O_SW), 0.0, ALU.mult, ALU.add)\
                    .then_inc(s["cs"], 1)
                dve.wait_ge(s["cs"], hp + 1)
                TT(cen(O_CC), cen(O_CS), bc(f(O_CS + CH // 2 - 1), (CH, NCH), (0, CH)), ALU.subtract)\
                    .then_inc(s["cc"], 1)

            def keys(hp):
                a = hp % 2
                kv = f(O_A + (KC + hp) * S)
                rv = f(O_A + hp * S)
                ar = lambda n: bc(f(O_AR + a * 2 * S + n * P, 2 * S - n * P), (2 * P, NT), (CH, 2), (1, CH))
                ep = lambda n: bc(f(O_EP + n, NCH * (CH + 1) - n), (2 * (CH + 1), NT), (CH + 1, 2), (1, CH))
                by_chunk = lambda off: bc(f(off), (P, NT), (CH, 2), (1, CH))
                read_out(dve, 1, "a", hp)
                TS(f(O_KS), f(O_SA), vec("k_a", hp), f(O_SM + 24 + hp, 1), ALU.mult, ALU.add).then_inc(s["kscale"], 1)
                dve.wait_ge(s["kk_ps"], hp + 1)
                free(TS(f(O_RN), banks[0][:, :], 1e-24, None, ALU.max), 0)
                dve.wait_ge(s["kscale"], hp + 1)
                TT(f(O_KS), f(O_KS), kv, ALU.mult).then_inc(s["kp"], 1)
                dve.wait_ge(s["ep"], hp + 1)
                TT(f(O_SM + 8 + a * 8, NCH - 1).rearrange("p (c o) -> p c o", o=1),
                   bc(f(O_EP + CH, NCH * (CH + 1) - CH), (CH + 1, NCH - 1), (1, 1)),
                   f(O_SM + 1, NCH - 1).rearrange("p (c o) -> p c o", o=1), ALU.mult).then_inc(s["scale"], 1)
                TT(ar(1), by_chunk(O_A + hp * S), ep(1), ALU.mult).then_inc(s["ar_r"], 1)
                dve.wait_ge(s["kp"], hp + 1)
                dve.wait_ge(s["em"], hp + 1)
                TT(f(O_KT + a * S), f(O_KS), f(O_EM), ALU.mult).then_inc(s["kt"], 1)
                STT(f(O_Q1), rv, vec("r_k", hp), f(O_KS), ALU.mult, ALU.mult).then_inc(s["rk"], 1)
                dve.wait_ge(s["kk_rs"], hp + 1)
                STT(f(O_KK), kv, vec("k_k", hp), f(O_RN), ALU.mult, ALU.mult).then_inc(s["kk"], 1)
                dve.wait_ge(s["kk"], hp + 1)
                TT(ar(0), by_chunk(O_KK), ep(0), ALU.mult).then_inc(s["ar_a"], 1)
                TT(f(O_SA), f(O_SA), f(O_KK), ALU.mult).then_inc(s["b_vec"], 1)
                dve.wait_ge(s["b_vec"], hp + 1)
                TT(f(O_BT + a * S), f(O_SA), f(O_EM), ALU.mult).then_inc(s["bt"], 1)
                dve.wait_ge(s["bonus_ps"], hp + 1)
                free(TT(f(O_BN + a * S), banks[1][:, :], xk(hp), ALU.mult), 1)

            def ub(h, n):
                return O_U + (h * 7 + n) * S

            def masked(hp, h, kind):
                for half in range(2):
                    b = 2 + 2 * h + half
                    dve.wait_ge(s[f"{kind}_sc{h}"], 2 * hp + half + 1)
                    for part, mask, to in ((0, C_STRICT, UB if kind == "b" else UK),
                                           (1, C_INCL, UR if kind == "b" else UKR)):
                        src = banks[b][:, :].rearrange("p (q a i) -> p q a i", q=2, a=2)[:, :, part, :]
                        ins = TT(bc(f(ub(h, to) + half * 2 * P, 2 * P), (P, 2), (1, P)), src,
                                 bc(f(O_CM + mask - C_STRICT, P), (0, 2), (1, P)), ALU.mult)
                        if part == 0 and kind == "b":
                            ins.then_inc(s[f"bm{h}"], 1)
                    free(ins, b)

            def x_masked(hp, h, n):
                b = 2 + 2 * h + (n == 0)
                dve.wait_ge(s[f"x_ps{h}"], N_LEV * hp + n + 1)
                lev = f(O_CM + C_LEV - C_STRICT + n * P, P)
                free(TT(bc(f(ub(h, UX if n else UT)), (P, NT), (1, P)),
                        banks[b][:, :].rearrange("p (q j) -> p q j", q=NT), bc(lev, (0, NT), (1, P)), ALU.mult), b)

            def transitions(hp, h):
                lo, a = HD * h, hp % 2
                for e in range(2):
                    b = 2 + 2 * h + e
                    dve.wait_ge(s[f"gh_ps{h}"], 2 * hp + e + 1)
                    ps = banks[b][lo:lo + HD, :].rearrange("p (q j) -> p q j", q=NT)
                    TT(bc(f(O_GT + e * P + lo, NCH * P - e * P - lo, lo, lo + HD), (2 * P, NT), (1, HD)), ps[:, :, 0:HD],
                       bc(f(O_CON + C_ID + lo, HD, lo, lo + HD), (0, NT), (1, HD)), ALU.add)
                    n = NT - e
                    free(TT(bc(f(O_HB + e * P + lo, NCH * P - e * P - lo, lo, lo + HD), (2 * P, n), (1, HD)),
                            ps[:, 0:n, HD:P],
                            bc(f(O_SM + 8 + a * 8 + e, 8 - e, lo, lo + HD), (2, n), (0, HD)), ALU.mult), b)

            def readout(hp, h):
                lo = HD * h
                dve.wait_ge(s[f"r2_ps{h}"], hp + 1)
                ar = f(O_AR + hp % 2 * 2 * S + P, 2 * S - P, lo, lo + HD)
                free(TT(f(O_R2, S, lo, lo + HD).rearrange("p (q i) -> p q i", q=NT),
                        banks[2 + 2 * h][lo:lo + HD, :].rearrange("p (q i) -> p q i", q=NT),
                        bc(ar, (2 * P, NT), (1, P)), ALU.add), 2 + 2 * h)

            def walk(hp):
                for c in range(1, NCH - 1):
                    dve.wait_ge(s["s_ps"], 6 * hp + c)
                    free(STT(f(O_SB + (c + 1) * P, P), banks[7][:, 0:P], f(O_SM + 8 + hp % 2 * 8 + c, 1),
                             f(O_HB + c * P, P), ALU.mult, ALU.add), 7)

            def finish(hp):
                dve.wait_ge(s["mean_ps"], hp + 1)
                if hp:
                    dve.wait_ge(s["yo_lo"], hp)
                free(TT(f(O_YC), f(O_Y), banks[0][:, :], ALU.subtract), 0)
                dve.wait_ge(s["y_rs"], hp + 1)
                TT(f(O_YC), f(O_YC), f(O_RS), ALU.mult).then_inc(s["y_step"], 1)
                dve.wait_ge(s["y_step"], 3 * hp + 1)
                TS(f(O_YC), f(O_YC), vec("ln_w", hp), vec("ln_b", hp), ALU.mult, ALU.add).then_inc(s["y_step"], 1)
                dve.wait_ge(s["y_step"], 3 * hp + 2)
                TT(f(O_YC), f(O_YC), f(O_BN + hp % 2 * S), ALU.add).then_inc(s["y_step"], 1)
                dve.wait_ge(s["y_step"], 3 * hp + 3)
                dve.wait_ge(s["g_ps"], hp + 1)
                TT(f(O_YC), f(O_YC), banks[0][:, :], ALU.mult).then_inc(s["bank0_free"], 1)
                dve.wait_ge(s["yo_hi"], hp + 1)
                TT(r(O_A + (KC + hp) * S), f(O_YC), rf(O_A + hp * S), ALU.subtract).then_inc(s["yo_lo"], 1)

            projected(dve)
            dve.wait_ge(s["mask_in"], 16)
            TS(f(O_SM + 24, KC), f(O_PV + VECS.index("k_a") * KC, KC), -1.0, 1.0, ALU.mult, ALU.add)\
                .then_inc(s["one_ka"], 1)
            dve.wait_ge(s["one_ka"], 1)
            decay_sums(0)
            keys(0)
            dve.wait_ge(s["zeroed"], 2)
            for hp in range(NHP):
                for h in range(2):
                    masked(hp, h, "b")
                for h in range(2):
                    masked(hp, h, "k")
                if hp < NHP - 1:
                    decay_sums(hp + 1)
                for n in range(N_LEV):
                    for h in range(2):
                        x_masked(hp, h, n)
                    if n == 3 and hp < NHP - 1:
                        keys(hp + 1)
                for h in range(2):
                    transitions(hp, h)
                for h in range(2):
                    readout(hp, h)
                walk(hp)
                finish(hp)

            def residual(n, t0):
                base = NORM_TMP[n]
                gain = ["ffn0", "mix1", "ffn1"][n]

                def low(m):
                    i = KC * n + m
                    dve.wait_ge(s["xg_hi"], i + 1)
                    TT(r(O_XG + (KC + m) * S), f(base + i % 2 * S), rf(O_XG + m * S), ALU.subtract)\
                        .then_inc(s["xg_lo"], 1)
                    add_squares(KC + i, base + (2 + i % 2) * S, NORM_ACC[n + 1], m == 0)

                for m in range(KC):
                    i = KC * n + m
                    split_low(p_of(t0 + m) + LEAD)
                    full(dve, t0 + m)
                    TT(xk(m), banks[(t0 + m) % 2][:, :], xk(m), ALU.add).then_inc(freed(t0 + m), 1)
                    dve.wait_ge(freed(t0 + m), (t0 + m) // 2 + 1)
                    if m >= 2:
                        dve.wait_ge(s["xg_lo"], i - 1)
                    TS(f(base + i % 2 * S), xk(m), vec(gain, m), None, ALU.mult).then_inc(s["xg_t"], 1)
                    if m:
                        low(m - 1)
                low(KC - 1)

            def feed_forward(n, t_in, t_out):
                def low(i):
                    dve.wait_ge(s["hd_hi"], FC * n + i + 1)
                    TT(r(O_HD + (FC + i) * S), f(O_FT + (6 + i % 2) * S), rf(O_HD + i * S), ALU.subtract)\
                        .then_inc(s["hd_lo"], 1)

                dve.wait_ge(s["rstd"], 2 * n + 2)
                for i in range(FC):
                    t, c = t_in + 2 * i, FC * n + i + 1
                    split_low(p_of(t) + LEAD)
                    full(dve, t)
                    TT(f(O_FT + i % 2 * S), banks[t % 2][:, :], f(O_RSTD), ALU.mult)\
                        .then_inc(freed(t), 1)
                    split_low(p_of(t + 1) + LEAD)
                    full(dve, t + 1)
                    TT(f(O_FT + (4 + i % 2) * S), banks[(t + 1) % 2][:, :], f(O_RSTD), ALU.mult)\
                        .then_inc(freed(t + 1), 1)
                    if i:
                        low(i - 1)
                    dve.wait_ge(s["silu"], c)
                    dve.wait_ge(freed(t + 1), (t + 1) // 2 + 1)
                    TT(f(O_FT + (6 + i % 2) * S), f(O_FT + (4 + i % 2) * S), f(O_FT + (2 + i % 2) * S), ALU.mult)\
                        .then_inc(s["hd"], 1)
                low(FC - 1)

            dve.wait_ge(s["x_again"], 16 * KC)
            residual(0, T_WO0)
            feed_forward(0, T_IN0, T_OUT0)
            residual(1, T_OUT0)

            def att_free(ins, b):
                ins.then_inc(s[f"bank{b}_free"], 1)

            def take_projection(hp, i):
                g, kind = divmod(i, 3)
                t = T_QKV + 9 * hp + i
                full(dve, t)
                if kind < 2:
                    n = 6 * hp + 2 * g + kind
                    if n >= 2:
                        dve.wait_ge(s["qk_norm"], n - 1)
                    out, in0, in1 = f(O_QR + n % 2 * S), banks[t % 2][:, :], f(O_RSTD)
                else:
                    if 3 * hp + g:
                        dve.wait_ge(s["aux_ps"], 9 * hp + i - 2)
                    out, in0, in1 = f(O_VR), banks[t % 2][:, :], f(O_RSTD)
                    if g:
                        out = by_residue(O_VR)
                        in0 = in0.rearrange("p (i r) -> p i r", r=4)
                        in1 = in1.rearrange("p (i r) -> p i r", r=4)
                TT(out, in0, in1, ALU.mult).then_inc(freed(t), 1)

            def by_residue(off):
                return bc(f(off), (1, P), (P, 4))

            def norm_projection(hp, i):
                g, kind = divmod(i, 3)
                if kind < 2:
                    n = 6 * hp + 2 * g + kind
                    dve.wait_ge(s["q_rs"], n + 1)
                    if hp >= 2 and g == 0:
                        dve.wait_ge(s["attended"], 8 * (hp - 1))
                    to = O_QN + (hp % 2 * 6 + g * 2 + kind) * S
                    gain = f(O_SM + 90 + g, 1) if kind == 0 else kol(len(VECS) * KC + 3 + g)
                    if g:
                        STT(by_residue(to), bc(f(O_QR + n % 2 * S), (4, P), (1, 4)), gain,
                            bc(f(O_QS), (4, P), (1, 4)), ALU.mult, ALU.mult).then_inc(s["qk_norm"], 1)
                    else:
                        STT(f(to), f(O_QR + n % 2 * S), gain, f(O_QS), ALU.mult, ALU.mult)\
                            .then_inc(s["qk_norm"], 1)

            def biased(hp, h, pair):
                b = 2 + pair % 2
                dve.wait_ge(s[f"logits{b}"], 4 * hp + 2 * h + pair // 2 + 1)
                dve.wait_ge(s[f"bias_in{h}"], 48 * (hp + 1))
                if hp:
                    dve.wait_ge(s["flipped"], 8 * (hp - 1) + 4 * h + 4)
                for e in range(2):
                    n = 2 * pair + e
                    first = P if n == 0 else 0
                    w = 2 * P - first
                    ins = V.tensor_tensor_reduce(
                        out=f(O_P + h * 4 * S + n * 2 * P + first, w), in0=banks[b][:, e * 2 * P + first:(e + 1) * 2 * P],
                        in1=f(O_BIAS + h * S + (0 if pair < 2 else 2 * P) + first, w), scale=1.0, scalar=-3.0e38,
                        op0=ALU.add, op1=ALU.max, accum_out=f(O_SM + 40 * h + n, 1))
                att_free(ins, b)

            def negate_max(hp, h, half):
                sm = O_SM + 40 * h + 4 * half
                att_read(dve, 3, (h, 2 * half + 1), hp)
                att_read(dve, 2, (h, 2 * half), hp)
                TS(f(sm + 8, 4), f(sm, 4), -1.0, None, ALU.mult).then_inc(s[f"neg_max{h}"], 1)

            def normalize(hp, h, half):
                sm = O_SM + 40 * h + 4 * half
                dve.wait_ge(s[f"exp{h}"], 8 * hp + 4 * half + 4)
                V.reciprocal(f(sm + 24, 4), f(sm + 16, 4)).then_inc(s["inv_sum"], 1)
                inv = 4 * hp + 2 * h + half + 1
                dve.wait_ge(s[f"log{h}"], 2 * hp + half + 1)
                if half:
                    TT(f(sm + 32, 4), f(sm + 8, 4), f(sm + 32, 4), ALU.subtract).then_inc(s[f"lse{h}"], 1)
                else:
                    TT(f(sm + 32, 4), f(sm, 4), f(sm + 32, 4), ALU.add).then_inc(s[f"lse{h}"], 1)
                dve.wait_ge(s["inv_sum"], inv)
                for n in range(4):
                    first = P if n == half == 0 else 0
                    tile = f(O_P + h * 4 * S + (4 * half + n) * 2 * P + first, 2 * P - first)
                    TS(tile, tile, f(sm + 24 + n, 1), None, ALU.mult).then_inc(s[f"probs{h}"], 1)

            def combine(hp):
                ob = banks[7][:, :].rearrange("p (r i) -> p i r", r=4)
                pr = lambda off: bc(f(off), (4, P), (1, 4))
                dve.wait_ge(s["attended"], 8 * (hp + 1))
                att_read(dve, 6, None, hp)
                TT(pr(O_DF), pr(O_OA), ob, ALU.subtract).then_inc(s["o_step"], 1)
                dve.wait_ge(s["o_step"], 2 * hp + 1)
                att_read(dve, 4, "lse", hp)
                TT(f(O_DF), f(O_DF), f(O_DW), ALU.mult).then_inc(s["o_step"], 1)
                dve.wait_ge(s["o_step"], 2 * hp + 2)
                att_free(TT(pr(O_DF), pr(O_DF), ob, ALU.add), 7)

            def combine_low(hp):
                dve.wait_ge(s["att_hi"], hp + 1)
                TT(r(O_O + (KC + hp) * S), f(O_DF), rf(O_O + hp * S), ALU.subtract).then_inc(s["att_lo"], 1)

            TS(f(O_SM + 90, 3), f(O_PV + len(VECS) * KC, 3), HD ** -0.5, None, ALU.mult).then_inc(s["q_gain"], 1)
            dve.wait_ge(s["q_gain"], 1)
            dve.wait_ge(s["rstd"], 3)
            for it in range(NHP + 1):
                a = it - 1
                for i in range(9):
                    if it < NHP:
                        split_low(p_of(T_QKV + 9 * it + i) + LEAD)
                        take_projection(it, i)
                        if i:
                            norm_projection(it, i - 1)
                    if a < 0:
                        continue
                    if i == 0 and a:
                        combine(a - 1)
                    if i < 4:
                        biased(a, i // 2, i % 2 * 2)
                        biased(a, i // 2, i % 2 * 2 + 1)
                        negate_max(a, i // 2, i % 2)
                    if i == 0 and a:
                        combine_low(a - 1)
                    if 1 <= i <= 4:
                        normalize(a, (i - 1) // 2, (i - 1) % 2)
            combine(NHP - 1)
            combine_low(NHP - 1)
            residual(2, T_WO1)
            feed_forward(1, T_IN1, T_OUT1)
            for m in range(KC):
                split_low(p_of(T_OUT1 + m) + LEAD)
                t = T_OUT1 + m
                full(dve, t)
                TT(xk(m), banks[t % 2][:, :], xk(m), ALU.add).then_inc(freed(t), 1)


        @block.gpsimd
        def _(pool):
            projected(pool)
            pool.memset(f(O_GT, NCH * P), 0.0).then_inc(s["zeroed"], 1)
            pool.memset(f(O_HB, NCH * P), 0.0).then_inc(s["zeroed"], 1)
            pool.wait_ge(s["mask_in"], 16)
            ident = bc(con(C_ID), (0, NT), (1, P))
            lev_t = bc(f(O_CM + C_LEVT - C_STRICT, P), (0, NT), (1, P))
            for hp in range(NHP):
                for h in range(2):
                    a, b = (bc(f(O_U + (h * 7 + n) * S), (P, NT), (1, P)) for n in (UB, UU))
                    pool.wait_ge(s[f"bm{h}"], 2 * (hp + 1))
                    nc.gpsimd.tensor_tensor(a, a, ident, ALU.add).then_inc(s[f"bi{h}"], 1)
                    pool.wait_ge(s[f"bi{h}"], hp + 1)
                    nc.gpsimd.tensor_tensor(b, a, lev_t, ALU.mult).then_inc(s[f"u0_{h}"], 1)


def kernel(**inputs):
    import concourse.bacc as bacc
    from concourse.bass_utils import run_bass_kernel_spmd as run

    a = {k: np.asarray(v) for k, v in inputs.items()}

    def tiles(w):
        k, m = w.shape
        return w.reshape(k // P, P, m // P, P).transpose(2, 0, 1, 3).reshape(-1, P, P)

    def padded(w, rows, cols):
        out = np.zeros((rows, cols), np.float32)
        out[:w.shape[0], :w.shape[1]] = w
        return out

    w_in = [a["ffn_w_in"][i].reshape(D, 2, FC, P).transpose(0, 2, 1, 3).reshape(D, 2 * F) for i in range(2)]
    qkv = a["attn_w_qkv"][0].reshape(D, 9, NHP, P).transpose(0, 2, 1, 3).reshape(D, 9 * D)
    g1 = padded(a["rwkv_g1"][0], D, 2 * P)
    parts = [a["rwkv_w_rkv"][0, 0], padded(a["rwkv_w1"][0], D, P), a["rwkv_w_rkv"][0, 1],
             padded(a["rwkv_a1"][0], D, P), a["rwkv_w_rkv"][0, 2], g1, a["rwkv_w_o"][0], w_in[0],
             a["ffn_w_out"][0], qkv, a["attn_w_o"][0], w_in[1], a["ffn_w_out"][1]]
    stream = np.concatenate([tiles(w) for w in parts])
    stream = np.ascontiguousarray(stream.reshape(N_PAN, 8, P, P).transpose(0, 2, 1, 3)).reshape(N_PAN, P, 8 * P)
    g2 = a["rwkv_g2"][0]
    lora = np.stack([padded(w, P, D) for w in (a["rwkv_w2"][0], a["rwkv_a2"][0], g2[:P], g2[P:])], axis=1)
    vecs = [a["mix_norm"][0], a["ffn_norm"][0], a["mix_norm"][1], a["ffn_norm"][1], *a["rwkv_mu"][0],
            a["rwkv_w0"][0], a["rwkv_a0"][0], a["rwkv_k_k"][0], a["rwkv_k_a"][0], a["rwkv_r_k"][0],
            a["rwkv_ln_w"][0], a["rwkv_ln_b"][0]]
    pvec = np.zeros((P, N_PV), np.float32)
    for i, v in enumerate(vecs):
        pvec[:, i * KC:(i + 1) * KC] = v.reshape(KC, P).T
    at = len(vecs) * KC
    for g in range(3):
        pvec[:, at + g] = np.tile(a["attn_q_gain"][0, g], 2)
        pvec[:, at + 3 + g] = np.tile(a["attn_k_gain"][0, g], 2)
    pvec[:, K_EPS], pvec[:, K_LNEPS], pvec[:, K_KKB] = 1e-6, 64e-5, 8 * math.log(2)
    pvec[:, K_ONE] = 1.0
    arrays = {
        "xT": np.ascontiguousarray(a["x"][0].T), "stream": stream, "lora_out": lora, "pvec": pvec,
        "const": shape_constants(), "rel33": np.concatenate([a["rel_bias"], np.ones((1, 48), np.float32)]),
    }
    nc = bacc.Bacc("TRN2", target_bir_lowering=False, num_devices=1)
    ins = [nc.dram_tensor(k, v.shape, mybir.dt.from_np(v.dtype), kind="ExternalInput").ap() for k, v in arrays.items()]
    out = nc.dram_tensor("outT", (D, S), F32, kind="ExternalOutput").ap()
    trunk(nc, *ins, out)
    got = run(nc, [arrays], core_ids=[0]).results[0]["outT"]
    return np.ascontiguousarray(got.T)[None]
```
